# Optimizing a Trainium2 kernel written in Bass

```python
import jax, jax.numpy as jnp
from jax import lax
import numpy as np

D_MODEL = 1024
BATCH = 1
SEQ = 1024
DEPTH = 1
DEC_BATCH = 8
DEC_SEQ = 1
PAST_LEN = 1024
PAGE_SIZE = 128

HEAD_DIM = 64
N_HEADS = 8
N_KV_HEADS = 2
GQA_GROUP = N_HEADS // N_KV_HEADS
WINDOW = 128
D_ATTN = N_HEADS * HEAD_DIM
D_KV = N_KV_HEADS * HEAD_DIM
D_LRU = 256
N_LRU_BLOCKS = 4
LRU_BLOCK = D_LRU // N_LRU_BLOCKS
LRU_CONV = 4
LRU_C = 8.0
D_SC = 256
SC_CONV = 3
D_MIX = D_ATTN + D_LRU + D_SC
D_IN = D_ATTN + 2 * D_KV + 2 * D_LRU + 3 * D_SC
D_FF = 2816
FFN_CONV = 3
EPS = 1e-6

kernel_name = "hymba_style_swa_rglru_shortconv_decoder_step"

def rmsnorm(x, g):
    xf = x.astype(jnp.float32)
    y = xf * lax.rsqrt(jnp.mean(xf * xf, axis=-1, keepdims=True) + EPS)
    return (y * g.astype(jnp.float32)).astype(x.dtype)

def causal_conv(buf, u, w):
    T = u.shape[1]
    K = w.shape[0]
    xp = jnp.concatenate([buf, u], axis=1)
    y = xp[:, 0:T] * w[0]
    for k in range(1, K):
        y = y + xp[:, k:k + T] * w[k]
    return y, xp[:, T:]

def sink_softmax(s, sink):
    m = jnp.maximum(jnp.max(s, axis=-1, keepdims=True), sink)
    p = jnp.exp(s - m)
    return p / (jnp.sum(p, axis=-1, keepdims=True) + jnp.exp(sink - m))

def attn_prompt(q, k, v, sinks):
    B, T, _ = q.shape
    nb = T // WINDOW
    qb = q.reshape(B, nb, WINDOW, N_KV_HEADS, GQA_GROUP, HEAD_DIM)
    kb = k.reshape(B, nb, WINDOW, N_KV_HEADS, HEAD_DIM)
    vb = v.reshape(B, nb, WINDOW, N_KV_HEADS, HEAD_DIM)
    pad = ((0, 0), (1, 0), (0, 0), (0, 0), (0, 0))
    kk = jnp.concatenate([jnp.pad(kb, pad)[:, :-1], kb], axis=2)
    vv = jnp.concatenate([jnp.pad(vb, pad)[:, :-1], vb], axis=2)
    s = jnp.einsum('bnqkgd,bnskd->bnkgqs', qb, kk).astype(jnp.float32) * (HEAD_DIM ** -0.5)
    qi = jnp.arange(WINDOW)[:, None] + WINDOW
    kj = jnp.arange(2 * WINDOW)[None, :]
    diff = qi - kj
    band = (diff >= 0) & (diff <= WINDOW)
    first = (jnp.arange(nb)[:, None, None] == 0) & (kj[None] < WINDOW)
    mask = band[None] & ~first
    s = jnp.where(mask[None, :, None, None], s, -jnp.inf)
    sink = sinks.reshape(N_KV_HEADS, GQA_GROUP)[:, :, None, None].astype(jnp.float32)
    p = sink_softmax(s, sink).astype(v.dtype)
    o = jnp.einsum('bnkgqs,bnskd->bnqkgd', p, vv).reshape(B, T, D_ATTN)
    k_new = k[:, -WINDOW:].reshape(B, WINDOW, N_KV_HEADS, HEAD_DIM)
    v_new = v[:, -WINDOW:].reshape(B, WINDOW, N_KV_HEADS, HEAD_DIM)
    return o, k_new, v_new

def attn_sample(q, k, v, cache_k, cache_v, sinks):
    B, T, _ = q.shape
    W = cache_k.shape[1]
    kk = jnp.concatenate([cache_k, k.reshape(B, T, N_KV_HEADS, HEAD_DIM)], axis=1)
    vv = jnp.concatenate([cache_v, v.reshape(B, T, N_KV_HEADS, HEAD_DIM)], axis=1)
    qg = q.reshape(B, T, N_KV_HEADS, GQA_GROUP, HEAD_DIM)
    s = jnp.einsum('btkgd,bskd->bkgts', qg, kk).astype(jnp.float32) * (HEAD_DIM ** -0.5)
    diff = (W + jnp.arange(T))[:, None] - jnp.arange(W + T)[None, :]
    mask = (diff >= 0) & (diff <= WINDOW)
    s = jnp.where(mask, s, -jnp.inf)
    sink = sinks.reshape(N_KV_HEADS, GQA_GROUP)[:, :, None, None].astype(jnp.float32)
    p = sink_softmax(s, sink).astype(v.dtype)
    o = jnp.einsum('bkgts,bskd->btkgd', p, vv).reshape(B, T, D_ATTN)
    return o, kk[:, -W:], vv[:, -W:]

def rglru(xc, h0, wa, ba, wi, bi, lam):
    B, T, _ = xc.shape
    xh = xc.reshape(B, T, N_LRU_BLOCKS, LRU_BLOCK)
    r = jax.nn.sigmoid(jnp.einsum('btnc,ncd->btnd', xh, wa).reshape(B, T, D_LRU) + ba)
    i = jax.nn.sigmoid(jnp.einsum('btnc,ncd->btnd', xh, wi).reshape(B, T, D_LRU) + bi)
    log_a = -LRU_C * r * jax.nn.softplus(-lam)
    a = jnp.exp(log_a)
    bx = jnp.sqrt(-jnp.expm1(2.0 * log_a)) * (i * xc)
    bx = bx.at[:, 0].add(a[:, 0] * h0)

    def combine(left, right):
        a1, b1 = left
        a2, b2 = right
        return a1 * a2, a2 * b1 + b2

    _, h = lax.associative_scan(combine, (a, bx), axis=1)
    return h, h[:, -1]

def decoder_layer(x, attn_cache, h0, lru_buf, sc_buf, ffn_buf,
                  g_mix, w_in, sinks, lru_conv_w, lru_conv_b, lru_wa, lru_ba, lru_wi, lru_bi,
                  lru_lambda, sc_conv_w, g_out, w_out, g_ffn, w_up, ffn_conv_w, w_down):
    h = rmsnorm(x, g_mix)
    z = h @ w_in
    cuts = np.cumsum([D_ATTN, D_KV, D_KV, D_LRU, D_LRU, D_SC, D_SC]).tolist()
    q, k, v, lru_x, lru_g, sc_b, sc_c, sc_u = jnp.split(z, cuts, axis=-1)
    if attn_cache is None:
        a_out, k_new, v_new = attn_prompt(q, k, v, sinks)
    else:
        a_out, k_new, v_new = attn_sample(q, k, v, attn_cache[0], attn_cache[1], sinks)
    xc, lru_buf_new = causal_conv(lru_buf, lru_x, lru_conv_w)
    hseq, h_last = rglru(xc + lru_conv_b, h0, lru_wa, lru_ba, lru_wi, lru_bi, lru_lambda)
    b_out = hseq * jax.nn.gelu(lru_g)
    sc_conv, sc_buf_new = causal_conv(sc_buf, sc_c * sc_u, sc_conv_w)
    c_out = sc_b * sc_conv
    merged = jnp.concatenate([
        rmsnorm(a_out, g_out[:D_ATTN]),
        rmsnorm(b_out, g_out[D_ATTN:D_ATTN + D_LRU]),
        rmsnorm(c_out, g_out[D_ATTN + D_LRU:])], axis=-1)
    x = x + merged @ w_out
    up = rmsnorm(x, g_ffn) @ w_up
    upc, ffn_buf_new = causal_conv(ffn_buf, up, ffn_conv_w)
    u, gt = jnp.split(upc, 2, axis=-1)
    x = x + (jax.nn.silu(gt) * u) @ w_down
    return x, (k_new, v_new, h_last, lru_buf_new, sc_buf_new, ffn_buf_new)

def setup_inputs(seed: int = 0) -> dict:
    key = jax.random.key(seed)
    ks = jax.random.split(key, 32)
    nrm = jax.random.normal
    f32 = jnp.float32
    win = min(WINDOW, PAST_LEN)
    u = jax.random.uniform(ks[20], (DEPTH, D_LRU), f32, 0.9, 0.999)
    s = u ** (1.0 / LRU_C)
    lam = jnp.log(s) - jnp.log1p(-s)
    return {
        "x_prompt": nrm(ks[0], (BATCH, SEQ, D_MODEL), f32),
        "x_sample": nrm(ks[1], (DEC_BATCH, DEC_SEQ, D_MODEL), f32),
        "cache_k": nrm(ks[2], (DEPTH, DEC_BATCH, win, N_KV_HEADS, HEAD_DIM), f32),
        "cache_v": nrm(ks[3], (DEPTH, DEC_BATCH, win, N_KV_HEADS, HEAD_DIM), f32),
        "state_rglru": 0.5 * nrm(ks[4], (DEPTH, DEC_BATCH, D_LRU), f32),
        "state_lru_conv": 0.5 * nrm(ks[5], (DEPTH, DEC_BATCH, LRU_CONV - 1, D_LRU), f32),
        "state_sconv": 0.5 * nrm(ks[6], (DEPTH, DEC_BATCH, SC_CONV - 1, D_SC), f32),
        "state_ffn_conv": 0.5 * nrm(ks[7], (DEPTH, DEC_BATCH, FFN_CONV - 1, 2 * D_FF), f32),
        "g_mix": 1.0 + 0.02 * nrm(ks[8], (DEPTH, D_MODEL), f32),
        "w_in": nrm(ks[9], (DEPTH, D_MODEL, D_IN), f32) * D_MODEL ** -0.5,
        "sinks": 0.5 * nrm(ks[10], (DEPTH, N_HEADS), f32),
        "lru_conv_w": nrm(ks[11], (DEPTH, LRU_CONV, D_LRU), f32) * LRU_CONV ** -0.5,
        "lru_conv_b": 0.01 * nrm(ks[12], (DEPTH, D_LRU), f32),
        "lru_wa": nrm(ks[13], (DEPTH, N_LRU_BLOCKS, LRU_BLOCK, LRU_BLOCK), f32) * LRU_BLOCK ** -0.5,
        "lru_ba": 0.01 * nrm(ks[14], (DEPTH, D_LRU), f32),
        "lru_wi": nrm(ks[15], (DEPTH, N_LRU_BLOCKS, LRU_BLOCK, LRU_BLOCK), f32) * LRU_BLOCK ** -0.5,
        "lru_bi": 0.01 * nrm(ks[16], (DEPTH, D_LRU), f32),
        "lru_lambda": lam,
        "sc_conv_w": nrm(ks[17], (DEPTH, SC_CONV, D_SC), f32) * SC_CONV ** -0.5,
        "g_out": 1.0 + 0.02 * nrm(ks[18], (DEPTH, D_MIX), f32),
        "w_out": nrm(ks[19], (DEPTH, D_MIX, D_MODEL), f32) * D_MIX ** -0.5,
        "g_ffn": 1.0 + 0.02 * nrm(ks[21], (DEPTH, D_MODEL), f32),
        "w_up": nrm(ks[22], (DEPTH, D_MODEL, 2 * D_FF), f32) * D_MODEL ** -0.5,
        "ffn_conv_w": nrm(ks[23], (DEPTH, FFN_CONV, 2 * D_FF), f32) * FFN_CONV ** -0.5,
        "w_down": nrm(ks[24], (DEPTH, D_FF, D_MODEL), f32) * D_FF ** -0.5,
        "g_final": 1.0 + 0.02 * nrm(ks[25], (D_MODEL,), f32),
    }

def _stack(states, i):
    return jnp.stack([s[i] for s in states])

def reference(x_prompt, x_sample, cache_k, cache_v, state_rglru, state_lru_conv, state_sconv,
              state_ffn_conv, g_mix, w_in, sinks, lru_conv_w, lru_conv_b, lru_wa, lru_ba,
              lru_wi, lru_bi, lru_lambda, sc_conv_w, g_out, w_out, g_ffn, w_up, ffn_conv_w,
              w_down, g_final):
    B = x_prompt.shape[0]
    dt = x_prompt.dtype
    h0_p = jnp.zeros((B, D_LRU), dt)
    lru_buf_p = jnp.zeros((B, LRU_CONV - 1, D_LRU), dt)
    sc_buf_p = jnp.zeros((B, SC_CONV - 1, D_SC), dt)
    ffn_buf_p = jnp.zeros((B, FFN_CONV - 1, 2 * D_FF), dt)
    xp, xs = x_prompt, x_sample
    p_states, s_states = [], []
    for l in range(DEPTH):
        lw = (g_mix[l], w_in[l], sinks[l], lru_conv_w[l], lru_conv_b[l], lru_wa[l], lru_ba[l],
              lru_wi[l], lru_bi[l], lru_lambda[l], sc_conv_w[l], g_out[l], w_out[l], g_ffn[l],
              w_up[l], ffn_conv_w[l], w_down[l])
        xp, sp = decoder_layer(xp, None, h0_p, lru_buf_p, sc_buf_p, ffn_buf_p, *lw)
        xs, ss = decoder_layer(xs, (cache_k[l], cache_v[l]), state_rglru[l], state_lru_conv[l],
                               state_sconv[l], state_ffn_conv[l], *lw)
        p_states.append(sp)
        s_states.append(ss)
    y_prompt = rmsnorm(xp, g_final)
    y_sample = rmsnorm(xs, g_final)
    new_cache_k_prompt = _stack(p_states, 0)
    new_cache_v_prompt = _stack(p_states, 1)
    new_state_rglru_prompt = _stack(p_states, 2)
    new_state_lru_conv_prompt = _stack(p_states, 3)
    new_state_sconv_prompt = _stack(p_states, 4)
    new_state_ffn_conv_prompt = _stack(p_states, 5)
    new_cache_k_sample = _stack(s_states, 0)
    new_cache_v_sample = _stack(s_states, 1)
    new_state_rglru_sample = _stack(s_states, 2)
    new_state_lru_conv_sample = _stack(s_states, 3)
    new_state_sconv_sample = _stack(s_states, 4)
    new_state_ffn_conv_sample = _stack(s_states, 5)
    return (y_prompt, y_sample,
            new_cache_k_prompt, new_cache_v_prompt, new_state_rglru_prompt,
            new_state_lru_conv_prompt, new_state_sconv_prompt, new_state_ffn_conv_prompt,
            new_cache_k_sample, new_cache_v_sample, new_state_rglru_sample,
            new_state_lru_conv_sample, new_state_sconv_sample, new_state_ffn_conv_sample)


_drawn_inputs = setup_inputs


def setup_inputs(seed=0):
    import zlib

    import numpy as np

    out = dict(_drawn_inputs(seed))
    spreads = {}
    factors = {'sinks': 8.0,
     'lru_ba': 8.0,
     'lru_bi': 8.0,
     'g_out': 29.919,
     'g_final': 21.907,
     'g_ffn': 7.19}
    for name, (base, spread) in spreads.items():
        noise = np.random.default_rng([zlib.crc32(name.encode()), seed]).standard_normal(out[name].shape)
        drawn = base * np.exp(spread * noise) if base else spread * noise
        out[name] = __import__('jax').numpy.asarray(drawn.astype(out[name].dtype))
    for name, factor in factors.items():
        out[name] = (out[name] * factor).astype(out[name].dtype)
    return out
```

```python
from contextlib import ExitStack

import numpy as np

import concourse.bass as bass
from concourse import mybir

F32 = mybir.dt.float32
F32R = mybir.dt.float32r
ALU = mybir.AluOpType
ACT = mybir.ActivationFunctionType

P = 128
D = 1024
KD = D // P
SEQ = 1024
NS = 8
T = SEQ + NS
NT = 3
TW = T // NT
LAST = TW - NS
HD = 64
G = 2
HG = 4
WIN = 128
NB = SEQ // WIN
FF = 2816
NF = FF // P
NG = NF // 2
EPS = 1e-6
SCALE = HD ** -0.5
MASKED = -1e30
C_LRU = 8.0

RAW, SPLIT = 3, 2
Z_SLOTS = 16
OUT_SLOT0 = Z_SLOTS
FFN_SLOT0 = OUT_SLOT0 + NT * KD
LOOP_SLOT0 = FFN_SLOT0 + 4
LOOPS = NG - 1
LAST_SLOT0 = LOOP_SLOT0 + 6 * LOOPS
N_SLOTS = LAST_SLOT0 + 2
OUT_JOB0 = NT * Z_SLOTS
FFN_JOB0 = OUT_JOB0 + NT * KD
LOOP_JOB0 = FFN_JOB0 + 12
ATT_JOB0 = 18
UNITS = NB * G
A_STEPS, B_STEPS = (36, 38, 39), (43, 45, 46)
PER_SLOT = 6

assert T % NT == 0 and TW % 2 == 0 and TW >= 256 and (PER_SLOT % RAW, PER_SLOT % SPLIT) == (0, 0)


def pe_tasks():
    after = {}

    def put(job, name, reader):
        after.setdefault(job, []).append((name, reader))

    for t in range(NT):
        put(t, ("norm", "x", t), "A")
    put(6, ("v", 0), "V")
    put(7, ("v", 1), "V")
    for i in range(2, UNITS + 2):
        put(ATT_JOB0 + i, ("pv", i - 2), "V")
    for k in range(4):
        put(ATT_JOB0 + k, ("sample", k), "V")
    for k in range(6):
        put(22 + k, ("gate", 0, k), "A")
        put(33 + k, ("gate", 1, k), "A")
    for t in range(NT):
        put(37 + t, ("norm", "A", t), "A")
        put(44 + t, ("norm", "B", t), "A")
    put(47, ("norm", "C", 0), "A")
    put(49, ("norm", "C", 1), "A")
    put(52, ("norm", "C", 2), "A")
    put(OUT_JOB0 + KD + 3, ("norm", "X", 0), "A")
    put(OUT_JOB0 + 2 * KD + 3, ("norm", "X", 1), "A")
    put(FFN_JOB0 + 1, ("norm", "X", 2), "A")
    for t in range(NT):
        put(FFN_JOB0 + 1000 + t, ("norm", "F", t), "A")
    return after


AFTER = pe_tasks()
ORDER = [task for job in sorted(AFTER) for task in AFTER[job]]
TASK = {name: n for n, (name, _) in enumerate(ORDER)}
NORMS = [name for name, _ in ORDER if name[0] == "norm"]


def done_at(name):
    return TASK[name] + 1


def read_at(name):
    n = TASK[name]
    return sum(reader == ORDER[n][1] for _, reader in ORDER[: n + 1])


class Link:

    def __init__(self, eng, sem):
        self.eng, self.sem, self.n, self.i, self.per = eng, sem, 0, None, 0

    def __call__(self, ins):
        ins.then_inc(self.sem, 1)
        self.n += 1
        self.eng.wait_ge(self.sem, self.n if self.i is None else self.i * self.per + self.n)

    def enter(self, i, per):
        self.i, self.per, self.start = i, per, self.n

    def leave(self, turns):
        assert self.n - self.start == self.per, (self.n - self.start, self.per)
        self.n, self.i = self.start + self.per * turns, None


def build(nc, dram, outs):
    ctx = ExitStack()
    with ctx:
        def sb(name, shape, dt=F32):
            return ctx.enter_context(nc.sbuf_tensor(name, shape, dt))

        def sem(name):
            return ctx.enter_context(nc.semaphore(name))

        x_sb = sb("x_sb", [P, KD, T])
        h_hi = sb("h_hi", [P, KD, T], F32R)
        h_lo = sb("h_lo", [P, KD, T], F32R)
        raw = [sb(f"raw{r}", [P, KD * P]) for r in range(RAW)]
        w_hi = [sb(f"w_hi{r}", [P, KD * P], F32R) for r in range(SPLIT)]
        w_lo = [sb(f"w_lo{r}", [P, KD * P], F32R) for r in range(SPLIT)]
        act_hi = [sb(f"act_hi{r}", [P, T], F32R) for r in range(2)]
        act_lo = [sb(f"act_lo{r}", [P, T], F32R) for r in range(2)]
        zb = sb("zb", [P, 11, T])
        q_sb = zb[:, 0:HG, :]
        k_sb = zb[:, 4, :]
        v_tok = zb[:, 5, 0:SEQ].rearrange("p (n d) -> p n d", n=NB)
        b_out = [zb[:, 6 + c, :] for c in range(2)]
        c_out = [zb[:, 8 + c, :] for c in range(2)]
        rstd = zb[:, 10, :]
        att = sb("att", [P, 3072])
        probs = [att[:, b * 1024:(b + 1) * 1024].rearrange("p (c k) -> p c k", c=HG) for b in range(2)]
        probs_t = att[:, 2048:3072].rearrange("p (s q) -> p s q", s=2)
        sq = att[:, 0:KD * TW].rearrange("p (k t) -> p k t", k=KD)
        n_const = 4 * KD + 8 + 2 * (4 + 1 + 1 + 1 + 1 + 3) + 2 * 8 * (3 + 1 + 2) + 2 + 2 * NF * 3
        const = sb("const", [P, n_const])
        at = [0]

        def cut(n):
            at[0] += n
            return const[:, at[0] - n:at[0]]

        gain_mix, gain_out, gain_ffn, gain_fin = (cut(KD) for _ in range(4))
        sinks = cut(8)
        lru_cw = cut(8).rearrange("p (c k) -> p c k", c=2)
        lru_cb, lru_ba, lru_bi, lru_lam = (cut(2) for _ in range(4))
        sc_cw = cut(6).rearrange("p (c k) -> p c k", c=2)
        lru_st = cut(48).rearrange("p (c b k) -> p c b k", c=2, b=NS)
        h0 = cut(16).rearrange("p (c b) -> p c b", c=2)
        sc_st = cut(32).rearrange("p (c b k) -> p c b k", c=2, b=NS)
        sink_s = cut(2)
        ffn_cw = cut(2 * NF * 3)
        ffn_st = sb("ffn_st", [P, 2 * NF * 16])
        ffn_tail = sb("ffn_tail", [P, 2 * NF * 2])
        ones = sb("ones", [P, P])
        ident = sb("ident", [P, P])
        half = sb("half", [P, 2])
        eps = sb("eps", [P, 1])
        small = sb("small", [P, 64])
        neg_max = [small[:, 4 * b:4 * b + 4] for b in range(2)]
        maxes = [small[:, 8 + 4 * b:12 + 4 * b] for b in range(2)]
        sink_exp = [small[:, 16 + 4 * b:20 + 4 * b] for b in range(2)]
        sums = [small[:, 24 + 4 * b:28 + 4 * b] for b in range(2)]
        c8 = small[:, 32:34]
        neg_c8 = small[:, 34:36]
        lam_t = small[:, 36:40]
        s_max, s_nmax, s_esink, s_sum = (small[0:32, 40 + 2 * i:42 + 2 * i] for i in range(4))
        h_stage = sb("h_stage", [P, 2, NS + 1])
        lru_stage = sb("lru_stage", [P, 2, 3 + 3 * NS])
        sc_stage = sb("sc_stage", [P, 2, 2 + 2 * NS])

        flat = x_sb[:, :, :].rearrange("p k t -> p (k t)")
        place = [0]

        def scratch(n):
            place[0] += n
            assert place[0] <= KD * T
            return flat[:, place[0] - n:place[0]]

        XP = SEQ + 3 + 4 * NS
        XC = XP - 3
        x_pad, conv_t, xc, r_a, vT = scratch(XP), scratch(XC), scratch(T), scratch(T), scratch(T)
        assert place[0] <= 6 * T - 300
        i_g, y_c = scratch(T), scratch(T)
        gate_w = scratch(4 * P)
        mask = scratch(2 * WIN)
        g_in = [y_c, vT]
        FREE_EARLY = 5
        PADC = SEQ + 2 + 3 * NS
        YC = PADC - 2
        s_scr = act_f = None
        ck = c_out[0][:, 0:NS * WIN].rearrange("p (b k) -> p b k", b=NS)
        cv = c_out[1][:, 0:NS * P].rearrange("p (b d) -> p b d", b=NS)
        s_qk = b_out[1][:, 0:32]
        s_t = b_out[1][:, 32:96]
        s_self = b_out[1][0:32, 96:98]
        s_sc = b_out[1][0:32, 100:100 + 2 * (WIN + 1)].rearrange("p (g k) -> p g k", g=G)
        s_diag = b_out[1][0:32, 360:424].rearrange("p (g r) -> p g r", g=G)
        s_pt = b_out[1][:, 424:488]
        s_bc = b_out[1][:, 488:520]
        zflat = zb[:, 0:10, :].rearrange("p k t -> p (k t)")
        pad_g, pad_u = zflat[:, 0:PADC], zflat[:, PADC:2 * PADC]
        y_g, y_u = zflat[:, 2200:2200 + YC], zflat[:, 3300:3300 + YC]
        act_f = zflat[:, 4400:4400 + T]

        psum = ctx.enter_context(nc.psum_tensor("psum", [P, 8 * 512], F32))
        job_ps = [psum[:, 512 * b:512 * b + TW] for b in range(3)]
        down_ps = [psum[:, 512 * (3 + b):512 * (3 + b) + TW] for b in range(4)]
        score_ps = psum[:, 3 * 512:5 * 512].rearrange("p (c k) -> p c k", c=HG)
        trans_ps = psum[:, 5 * 512:7 * 512].rearrange("p (s q) -> p s q", s=2)
        task_ps = psum[:, 7 * 512:8 * 512]

        raw_landed = [sem(f"raw_landed{r}") for r in range(RAW)]
        x_landed = [sem(f"x_landed{t}") for t in range(NT)]
        x_back = [sem(f"x_back{m}") for m in range(KD)]
        const_landed = sem("const_landed")
        gate_landed = sem("gate_landed")
        cache_landed = sem("cache_landed")
        gate_zeroed = sem("gate_zeroed")
        w_hi_ready, w_lo_ready, w_lo2_ready, w_used = sem("w_hi_ready"), sem("w_lo_ready"), sem("w_lo2_ready"), sem("w_used")
        h_hi_ready, h_ready = sem("h_hi_ready"), sem("h_ready")
        job_done, job_read = sem("job_done"), sem("job_read")
        task_done, read_a, read_v = sem("task_done"), sem("read_a"), sem("read_v")
        sq_ready, sq_sum_ready = sem("sq_ready"), sem("sq_sum_ready")
        consts_made = sem("consts_made")
        pe_link = sem("pe_link")
        v_link, a_link, p_link = sem("v_link"), sem("a_link"), sem("p_link")
        lam_ready, c8_ready = sem("lam_ready"), sem("c8_ready")
        scores_done, scores_read = sem("scores_done"), sem("scores_read")
        neg_max_ready, exp_done, probs_ready = sem("neg_max_ready"), sem("exp_done"), sem("probs_ready")
        trans_done, probs_t_ready = sem("trans_done"), sem("probs_t_ready")
        s_ready, s_neg_ready, s_exp_done = sem("s_ready"), sem("s_neg_ready"), sem("s_exp_done")
        xc_ready, decay_ready, bx_ready, root_done, gelu_done = sem("xc_ready"), sem("decay_ready"), sem("bx_ready"), sem("root_done"), sem("gelu_done")
        att_ready, b_ready, c_ready, ab_ready, cm_ready = sem("att_ready"), sem("b_ready"), sem("c_ready"), sem("ab_ready"), sem("cm_ready")
        scratch_free = sem("scratch_free")
        conv_g_ready, silu_done, act_ready, act_hi_ready, act_split = sem("conv_g_ready"), sem("silu_done"), sem("act_ready"), sem("act_hi_ready"), sem("act_split")
        down_done, down_read = sem("down_done"), sem("down_read")
        y_ready = sem("y_ready")
        stage_ready, stored, kv_stored = sem("stage_ready"), sem("stored"), sem("kv_stored")

        def tile(t):
            return slice(t * TW, (t + 1) * TW)

        def f32(ap):
            return ap.bitcast(F32)

        block = ctx.enter_context(nc.Block())

        @block.sync
        def _(sp):
            w_dram = dram["w"]

            def load_slot(s, index, turn=None):
                if s >= RAW:
                    used = s - RAW + 1 if turn is None else turn * PER_SLOT + (s - RAW + 1)
                    sp.wait_ge(w_hi_ready, used)
                    sp.wait_ge(w_lo_ready, used)
                src = w_dram[index] if turn is None else w_dram[bass.ds(turn * PER_SLOT + index, 1)].rearrange("a p n -> (a p) n")
                sp.dma_start(raw[s % RAW][:, :], src).then_inc(raw_landed[s % RAW], 16)

            for t in range(NT):
                sp.dma_start(x_sb[:, :, tile(t)], dram["x"][:, :, tile(t)]).then_inc(x_landed[t], 16)
                if t == 0:
                    load_slot(0, 0)
            for s in range(1, Z_SLOTS):
                load_slot(s, s)
            for s in range(OUT_SLOT0, FFN_SLOT0 + RAW):
                if s - RAW >= OUT_SLOT0:
                    sp.wait_ge(w_lo2_ready, s - RAW - OUT_SLOT0 + 1)
                load_slot(s, Z_SLOTS + (s - OUT_SLOT0) % KD if s < FFN_SLOT0 else s - OUT_SLOT0)
            for s in range(FFN_SLOT0 + RAW, LOOP_SLOT0):
                load_slot(s, s - OUT_SLOT0)
            with sp.Fori(0, LOOPS) as i:
                for c in range(PER_SLOT):
                    load_slot(LOOP_SLOT0 + c, LOOP_SLOT0 + c - OUT_SLOT0, i)
            for s in range(LAST_SLOT0, N_SLOTS):
                load_slot(s, s - OUT_SLOT0)
            sp.wait_ge(act_split, NF)
            sp.dma_start(outs["ffn_tail"], ffn_tail[:, :]).then_inc(stored, 16)
            sp.dma_start(outs["ffn_sample"], ffn_st[:, :]).then_inc(stored, 16)
            for t in range(NT):
                sp.wait_ge(y_ready, t + 1)
                sp.dma_start(outs["y"][:, :, tile(t)], x_sb[:, :, tile(t)]).then_inc(stored, 16)
            sp.wait_ge(kv_stored, 16 * 2)
            sp.wait_ge(stored, 16 * (7 + NT))

        @block.gpsimd
        def _(pool):
            link = Link(pool, p_link)
            nc.gpsimd.memset(ones[:, :], 1.0).then_inc(consts_made, 1)
            nc.gpsimd.memset(eps[:, :], EPS).then_inc(consts_made, 1)
            link(nc.gpsimd.memset(ident[:, :], 0.0))
            nc.gpsimd.affine_select(out=ident[:, :], in_=ident[:, :], compare_op=ALU.not_equal, fill=1.0,
                                    base=0, pattern=[[-1, P]], channel_multiplier=1).then_inc(consts_made, 1)
            link(nc.gpsimd.memset(half[:, :], 1.0))
            link(nc.gpsimd.affine_select(out=half[:, 0:1], in_=half[:, 0:1], compare_op=ALU.is_gt, fill=0.0,
                                         base=HD, pattern=[[0, 1]], channel_multiplier=-1))
            nc.gpsimd.affine_select(out=half[:, 1:2], in_=half[:, 1:2], compare_op=ALU.is_ge, fill=0.0,
                                    base=-HD, pattern=[[0, 1]], channel_multiplier=1).then_inc(consts_made, 1)

            def lo(s, turn=None, width=KD * P):
                n = s + 1 if turn is None else turn * PER_SLOT + (s + 1)
                pool.wait_ge(w_hi_ready, n)
                nc.gpsimd.tensor_tensor(w_lo[s % SPLIT][:, 0:width], raw[s % RAW][:, 0:width],
                                        f32(w_hi[s % SPLIT][:, 0:width]), ALU.subtract).then_inc(w_lo_ready, 1)

            lo(0)
            lo(1)
            pool.wait_ge(h_ready, NT)
            pool.wait_ge(sq_ready, NT)
            link(nc.gpsimd.memset(mask, 0.0))
            link(nc.gpsimd.affine_select(out=mask[:, 0:WIN], in_=mask[:, 0:WIN], compare_op=ALU.is_ge, fill=MASKED,
                                         base=0, pattern=[[1, WIN]], channel_multiplier=-1))
            nc.gpsimd.affine_select(out=mask[:, WIN:], in_=mask[:, WIN:], compare_op=ALU.is_ge, fill=MASKED,
                                    base=0, pattern=[[-1, WIN]], channel_multiplier=1).then_inc(consts_made, 1)
            nc.gpsimd.memset(gate_w, 0.0).then_inc(gate_zeroed, 1)
            for s in range(2, Z_SLOTS):
                lo(s)
            for s in range(OUT_SLOT0, FFN_SLOT0):
                lo(s, width=KD * P // 2)
            for s in range(FFN_SLOT0, LOOP_SLOT0):
                lo(s)
            with pool.Fori(0, LOOPS) as i:
                for c in range(PER_SLOT):
                    lo(LOOP_SLOT0 + c, i)
            for s in range(LAST_SLOT0, N_SLOTS):
                lo(s)

        @block.scalar
        def _(act):
            link = Link(act, a_link)

            def hi(s, turn=None):
                if turn is None:
                    act.wait_ge(raw_landed[s % RAW], 16 * (s // RAW + 1))
                    if s >= SPLIT:
                        act.wait_ge(w_used, s - SPLIT + 1)
                else:
                    act.wait_ge(raw_landed[s % RAW], turn * (16 * PER_SLOT // RAW) + 16 * (s // RAW + 1))
                    act.wait_ge(w_used, turn * PER_SLOT + (s - SPLIT + 1))
                nc.scalar.activation(w_hi[s % SPLIT][:, :], raw[s % RAW][:, :], ACT.Copy).then_inc(w_hi_ready, 1)

            def square(name, src, n):
                k = NORMS.index(name)
                if k:
                    act.wait_ge(task_done, done_at(NORMS[k - 1]))
                nc.scalar.activation(sq[:, 0:n, :], src, ACT.Square).then_inc(sq_ready, 1)

            def root(name, dst, width):
                act.wait_ge(task_done, done_at(name))
                nc.scalar.activation(dst, task_ps[:, 0:TW], ACT.Sqrt, bias=eps[:, 0:1],
                                     scale=1.0 / width).then_inc(read_a, 1)

            for name, dst in (("const", const[:, :]), ("ffn_state", ffn_st[:, :])):
                act.dma_start(dst, dram[name]).then_inc(const_landed, 16)
            act.dma_start(ck, dram["ck"]).then_inc(cache_landed, 16)
            act.dma_start(cv, dram["cv"]).then_inc(cache_landed, 16)
            act.dma_start(outs["k_old"], dram["k_keep"]).then_inc(stored, 16)
            act.dma_start(outs["v_old"], dram["v_keep"]).then_inc(stored, 16)
            act.wait_ge(const_landed, 32)
            act.wait_ge(consts_made, 2)
            for t in range(NT):
                act.wait_ge(x_landed[t], 16)
                for k in range(KD):
                    ins = nc.scalar.activation(h_hi[:, k, tile(t)], x_sb[:, k, tile(t)], ACT.Copy,
                                               scale=gain_mix[:, k:k + 1])
                ins.then_inc(h_hi_ready, 1)
                if t == 0:
                    hi(0)
                square(("norm", "x", t), x_sb[:, :, tile(t)], KD)
                if t == 0:
                    hi(1)
                if t:
                    root(("norm", "x", t - 1), rstd[:, tile(t - 1)], D)
            root(("norm", "x", 2), rstd[:, tile(2)], D)
            act.wait_ge(lam_ready, 1)
            link(nc.scalar.activation(lam_t[:, 2:4], lam_t[:, 0:2], ACT.Exp, scale=-1.0))
            nc.scalar.activation(lam_t[:, 2:4], lam_t[:, 2:4], ACT.Ln, bias=1.0).then_inc(lam_ready, 1)
            act.wait_ge(gate_zeroed, 1)
            for b in range(4):
                for w in range(2):
                    o = (b % 2) * HD
                    col = (w * 2 + b // 2) * P + o
                    act.dma_start(gate_w[o:o + HD, col:col + HD], dram["gate_w"][w, b]).then_inc(gate_landed, 16)

            def exps(u):
                act.wait_ge(neg_max_ready, u + 1)
                b, low = u % 2, WIN if u < G else 0
                for c in range(HG):
                    nc.scalar.activation(probs[b][:, c, low:], probs[b][:, c, low:], ACT.Exp,
                                         bias=neg_max[b][:, c:c + 1], accum_out=sums[b][:, c:c + 1])
                nc.scalar.activation(sink_exp[b], sink_exp[b], ACT.Exp).then_inc(exp_done, 1)

            def probs_t_copy(u):
                act.wait_ge(trans_done, u + 1)
                if u:
                    act.wait_ge(task_done, done_at(("pv", u - 1)))
                if u >= G:
                    nc.scalar.activation(probs_t[:, 0, :], trans_ps[:, 0, :], ACT.Copy)
                nc.scalar.activation(probs_t[:, 1, :], trans_ps[:, 1, :], ACT.Copy).then_inc(probs_t_ready, 1)

            def gate(c, k):
                act.wait_ge(task_done, done_at(("gate", c, k)))
                dst = (r_a, i_g)[k // 3]
                nc.scalar.activation(dst[:, tile(k % 3)], task_ps[:, 0:TW], ACT.Sigmoid,
                                     bias=(lru_ba, lru_bi)[k // 3][:, c:c + 1]).then_inc(read_a, 1)

            def decays(c):
                act.wait_ge(c8_ready, 2)
                act.wait_ge(read_a, read_at(("gate", c, 2)))
                nc.scalar.activation(conv_t[:, 0:T], r_a, ACT.Tanh, scale=c8[:, c:c + 1])
                nc.scalar.activation(r_a, r_a, ACT.Exp, scale=neg_c8[:, c:c + 1]).then_inc(decay_ready, 1)

            for j in range(3, OUT_JOB0):
                i = j - ATT_JOB0
                if 2 <= i < UNITS + 2:
                    probs_t_copy(i - 2)
                if 0 <= i < UNITS:
                    exps(i)
                if j == ATT_JOB0 + 1:
                    act.wait_ge(s_neg_ready, 1)
                    for g in range(G):
                        nc.scalar.activation(s_sc[:, g, :], s_sc[:, g, :], ACT.Exp, bias=s_nmax[:, g:g + 1],
                                             accum_out=s_sum[:, g:g + 1])
                    nc.scalar.activation(s_esink, s_esink, ACT.Exp).then_inc(s_exp_done, 1)
                if j in (24, 30):
                    c = (j - 24) // 6
                    act.wait_ge(job_read, 24 + 6 * c)
                    nc.scalar.activation(g_in[c], g_in[c], ACT.Gelu_apprx_tanh).then_inc(gelu_done, 1)
                if j in (28, 39):
                    decays((j - 28) // 11)
                if j in (30, 41):
                    c = (j - 30) // 11
                    act.wait_ge(bx_ready, c + 1)
                    nc.scalar.activation(conv_t[:, 0:T], conv_t[:, 0:T], ACT.Sqrt).then_inc(root_done, 1)
                if j in A_STEPS:
                    act.wait_ge(att_ready, UNITS)
                    act.wait_ge(kv_stored, 16 * 2)
                    square(("norm", "A", A_STEPS.index(j)), q_sb[:, :, tile(A_STEPS.index(j))], HG)
                if j in B_STEPS:
                    act.wait_ge(b_ready, 2)
                    square(("norm", "B", B_STEPS.index(j)), zb[:, 6:8, tile(B_STEPS.index(j))], 2)
                if j == 47:
                    act.wait_ge(c_ready, 1)
                    square(("norm", "C", 0), zb[:, 8:10, tile(0)], 2)
                if j == 46:
                    act.wait_ge(scratch_free, 1)
                    for m in range(FREE_EARLY):
                        act.dma_start(x_sb[:, m, :], dram["x"][:, m, :]).then_inc(x_back[m], 16)
                if j % 3 == 0:
                    hi(j // 3 + 1)
                for name, reader in AFTER.get(j, []):
                    if name[0] == "gate":
                        gate(name[1], name[2])
                    if name[0] == "norm" and name[1] == "A":
                        root(name, k_sb[:, tile(name[2])], HG * P)
                    if name[0] == "norm" and name[1] == "B":
                        root(name, zb[:, 5, tile(name[2])], 2 * P)
                if j == 20:
                    act.wait_ge(job_read, 6)
                    act.dma_start(outs["k_new"], k_sb[:, SEQ - WIN:]).then_inc(kv_stored, 16)
                    act.dma_start(outs["v_new"], vT[:, SEQ - WIN:]).then_inc(kv_stored, 16)
                if j == 46:
                    act.wait_ge(stage_ready, 1)
                    for nm, src in (("h_last", h_stage), ("lru_state", lru_stage), ("sc_state", sc_stage)):
                        act.dma_start(outs[nm], src[:, :, :]).then_inc(stored, 16)

            def merged_ab(t):
                act.wait_ge(ab_ready, 6)
                act.wait_ge(job_done, OUT_JOB0 - NT + t + 1)
                for k in range(6):
                    ins = nc.scalar.activation(h_hi[:, k, tile(t)], zb[:, (k if k < 4 else k + 2), tile(t)], ACT.Copy)
                ins.then_inc(h_hi_ready, 1)

            def merged_c(t):
                root(("norm", "C", t), k_sb[:, tile(t)], 2 * P)
                act.wait_ge(cm_ready, t + 1)
                for k in range(2):
                    ins = nc.scalar.activation(h_hi[:, 6 + k, tile(t)], c_out[k][:, tile(t)], ACT.Copy)
                ins.then_inc(h_hi_ready, 1)

            merged_ab(0)
            act.wait_ge(c_ready, NT)
            for m in range(FREE_EARLY, KD):
                act.dma_start(x_sb[:, m, :], dram["x"][:, m, :]).then_inc(x_back[m], 16)
            merged_c(0)
            for j in range(NT * KD):
                hi(OUT_SLOT0 + j + 1)
                if j == 0:
                    square(("norm", "C", 1), zb[:, 8:10, tile(1)], 2)
                    merged_ab(1)
                if j == 1:
                    merged_c(1)
                if j == 3:
                    square(("norm", "C", 2), zb[:, 8:10, tile(2)], 2)
                    merged_ab(2)
                if j == 4:
                    merged_c(2)
                if j in (KD + 1, 2 * KD + 1):
                    x2_split_hi(nc, act, j // KD - 1, h_hi, x_sb, gain_ffn, tile, job_read, h_hi_ready)
                    square(("norm", "X", j // KD - 1), x_sb[:, :, tile(j // KD - 1)], KD)
                if j in (KD + 3, 2 * KD + 3):
                    root(("norm", "X", j // KD - 1), rstd[:, tile(j // KD - 1)], D)
            x2_split_hi(nc, act, 2, h_hi, x_sb, gain_ffn, tile, job_read, h_hi_ready)
            square(("norm", "X", 2), x_sb[:, :, tile(2)], KD)

            def silu(n, i=None):
                act.wait_ge(conv_g_ready, n + 1 if i is None else i * 2 + (n + 1))
                nc.scalar.activation(y_g, y_g, ACT.Silu).then_inc(silu_done, 1)

            def split_act(n, downs, i=None):
                act.wait_ge(act_ready, n + 1 if i is None else i * 2 + (n + 1))
                if downs is not None:
                    act.wait_ge(down_done, downs if i is None else i * 24 + downs)
                nc.scalar.activation(act_hi[n % 2][:, :], act_f, ACT.Copy).then_inc(act_hi_ready, 1)

            hi(FFN_SLOT0 + 1)
            root(("norm", "X", 2), rstd[:, tile(2)], D)
            hi(FFN_SLOT0 + 2)
            silu(0)
            split_act(0, None)
            hi(FFN_SLOT0 + 3)
            hi(FFN_SLOT0 + 4)
            silu(1)
            split_act(1, None)
            with act.Fori(0, LOOPS) as i:
                hi(LOOP_SLOT0 + 1, i)
                hi(LOOP_SLOT0 + 2, i)
                silu(2, i)
                hi(LOOP_SLOT0 + 3, i)
                hi(LOOP_SLOT0 + 4, i)
                split_act(2, 24, i)
                hi(LOOP_SLOT0 + 5, i)
                hi(LOOP_SLOT0 + 6, i)
                silu(3, i)
                split_act(3, 24, i)
            hi(LAST_SLOT0 + 1)
            for t in range(NT):
                act.wait_ge(down_read, 24 * LOOPS + 12 + 4 * (t + 1))
                square(("norm", "F", t), x_sb[:, :, tile(t)], KD)
                root(("norm", "F", t), rstd[:, tile(t)], D)

        @block.vector
        def _(dve):
            V = nc.vector
            link = Link(dve, v_link)

            def sq_tree(name, n):
                dve.wait_ge(sq_ready, NORMS.index(name) + 1)
                while n > 2:
                    n //= 2
                    link(V.tensor_tensor(sq[:, 0:n, :], sq[:, 0:n, :], sq[:, n:2 * n, :], ALU.add))
                V.tensor_tensor(sq[:, 0, :], sq[:, 0, :], sq[:, 1, :], ALU.add).then_inc(sq_sum_ready, 1)

            def reciprocal(name, dst):
                dve.wait_ge(read_a, read_at(name))
                link(V.reciprocal(dst, dst))

            dve.wait_ge(const_landed, 32)
            V.scalar_tensor_tensor(out=lam_t[:, 0:2], in0=lru_lam, scalar=-1.0, in1=lru_lam, op0=ALU.mult, op1=ALU.max).then_inc(lam_ready, 1)
            for t in range(NT):
                dve.wait_ge(h_hi_ready, t + 1)
                for k in range(KD):
                    ins = V.scalar_tensor_tensor(out=h_lo[:, k, tile(t)], in0=x_sb[:, k, tile(t)],
                                                 scalar=gain_mix[:, k:k + 1], in1=f32(h_hi[:, k, tile(t)]),
                                                 op0=ALU.mult, op1=ALU.subtract)
                ins.then_inc(h_ready, 1)
                sq_tree(("norm", "x", t), KD)
                if t:
                    reciprocal(("norm", "x", t - 1), rstd[:, tile(t - 1)])
            reciprocal(("norm", "x", 2), rstd[:, tile(2)])
            dve.wait_ge(lam_ready, 2)
            link(V.tensor_scalar(lam_t[:, 0:2], lru_lam, -1.0, 0.0, ALU.mult, ALU.max))
            link(V.tensor_tensor(c8, lam_t[:, 0:2], lam_t[:, 2:4], ALU.add))
            link(V.tensor_scalar(c8, c8, C_LRU, None, ALU.mult))
            V.tensor_scalar(neg_c8, c8, -1.0, None, ALU.mult).then_inc(c8_ready, 2)

            def evac(j, dst, sample_dst=None):
                t = j % NT
                dve.wait_ge(job_done, j + 1)
                src, scale = job_ps[t], rstd[:, tile(t)]
                if sample_dst is None or t < NT - 1:
                    V.tensor_tensor(dst[:, tile(t)], src, scale, ALU.mult).then_inc(job_read, 1)
                else:
                    V.tensor_tensor(dst[:, t * TW:SEQ], src[:, 0:LAST], scale[:, 0:LAST], ALU.mult)
                    V.tensor_tensor(sample_dst, src[:, LAST:], scale[:, LAST:], ALU.mult).then_inc(job_read, 1)

            def samples(pad, k):
                return pad[:, SEQ + k - 1:SEQ + k - 1 + k * NS].rearrange("p (b k) -> p b k", b=NS)

            def conv_lru(c):
                dve.wait_ge(job_read, 21 + 6 * c)
                s = samples(x_pad, 4)
                V.tensor_copy(lru_stage[:, c, 0:3], x_pad[:, SEQ:SEQ + 3])
                V.tensor_copy(lru_stage[:, c, 3:].rearrange("p (b k) -> p b k", b=NS), s[:, :, 1:4])
                link(V.tensor_scalar(conv_t, x_pad[:, 0:XC], lru_cw[:, c, 0:1], lru_cb[:, c:c + 1], ALU.mult, ALU.add))
                for k in (1, 2):
                    link(V.scalar_tensor_tensor(out=conv_t, in0=x_pad[:, k:k + XC], scalar=lru_cw[:, c, k:k + 1],
                                                in1=conv_t, op0=ALU.mult, op1=ALU.add))
                V.scalar_tensor_tensor(out=xc[:, 0:SEQ], in0=x_pad[:, 3:3 + SEQ], scalar=lru_cw[:, c, 3:4],
                                       in1=conv_t[:, 0:SEQ], op0=ALU.mult, op1=ALU.add)
                V.scalar_tensor_tensor(out=xc[:, SEQ:], in0=s[:, :, 3], scalar=lru_cw[:, c, 3:4],
                                       in1=conv_t[:, SEQ + 3:XC:4], op0=ALU.mult, op1=ALU.add).then_inc(xc_ready, 1)

            def gate_input(c):
                dve.wait_ge(read_a, read_at(("gate", c, 5)))
                link(V.tensor_tensor(i_g, i_g, xc, ALU.mult))

            def lru_root(c):
                dve.wait_ge(decay_ready, c + 1)
                link(V.tensor_tensor(b_out[c], r_a, r_a, ALU.mult))
                V.scalar_tensor_tensor(out=conv_t[:, 0:T], in0=b_out[c], scalar=1.0, in1=conv_t[:, 0:T],
                                       op0=ALU.add, op1=ALU.mult).then_inc(bx_ready, 1)

            def lru_scan(c):
                dve.wait_ge(root_done, c + 1)
                link(V.tensor_tensor(i_g, i_g, conv_t[:, 0:T], ALU.mult))
                V.tensor_tensor_scan(b_out[c][:, 0:SEQ], r_a[:, 0:SEQ], i_g[:, 0:SEQ], 0.0, ALU.mult, ALU.add)
                link(V.tensor_tensor(b_out[c][:, SEQ:], r_a[:, SEQ:], h0[:, c, :], ALU.mult))
                link(V.tensor_tensor(b_out[c][:, SEQ:], b_out[c][:, SEQ:], i_g[:, SEQ:], ALU.add))
                link(V.tensor_copy(h_stage[:, c, :], b_out[c][:, SEQ - 1:]))
                dve.wait_ge(gelu_done, c + 1)
                V.tensor_tensor(b_out[c], b_out[c], g_in[c], ALU.mult).then_inc(b_ready, 1)

            def conv3(pad, w, tmp, out):
                link(V.tensor_scalar(tmp, pad[:, 0:YC], w(0), None, ALU.mult))
                link(V.scalar_tensor_tensor(out=tmp, in0=pad[:, 1:1 + YC], scalar=w(1), in1=tmp,
                                            op0=ALU.mult, op1=ALU.add))
                V.scalar_tensor_tensor(out=out[:, 0:SEQ], in0=pad[:, 2:2 + SEQ], scalar=w(2), in1=tmp[:, 0:SEQ],
                                       op0=ALU.mult, op1=ALU.add)
                return V.scalar_tensor_tensor(out=out[:, SEQ:], in0=samples(pad, 3)[:, :, 2], scalar=w(2),
                                              in1=tmp[:, SEQ + 2:YC:3], op0=ALU.mult, op1=ALU.add)

            pad3 = x_pad[:, 0:PADC]

            def sc_product(c, t):
                dve.wait_ge(job_read, 36 + 9 * c - 2 + t)
                n = TW if t < NT - 1 else LAST
                dst = pad3[:, 2 + t * TW:2 + t * TW + n]
                ins = V.tensor_tensor(dst, dst, c_out[c][:, t * TW:t * TW + n], ALU.mult)
                if t == NT - 1:
                    link(ins)
                    s = samples(pad3, 3)[:, :, 2]
                    link(V.tensor_tensor(s, s, c_out[c][:, SEQ:], ALU.mult))

            def sc_conv(c):
                V.tensor_copy(sc_stage[:, c, 0:2], pad3[:, SEQ:SEQ + 2])
                stage = V.tensor_copy(sc_stage[:, c, 2:].rearrange("p (b k) -> p b k", b=NS), samples(pad3, 3)[:, :, 1:3])
                if c:
                    stage.then_inc(stage_ready, 1)
                link(conv3(pad3, lambda k: sc_cw[:, c, k:k + 1], conv_t[:, 0:YC], y_c))

            def score_max(u):
                b, g, low = u % 2, u % G, WIN if u < G else 0
                dve.wait_ge(scores_done, u + 1)
                if u == 0:
                    dve.wait_ge(consts_made, 5)
                if u >= 2:
                    dve.wait_ge(trans_done, u - 1)
                for c in range(HG):
                    h = g * HG + c
                    ins = V.tensor_tensor_reduce(probs[b][:, c, low:], score_ps[:, c, low:], mask[:, low:], SCALE,
                                                 sinks[:, h:h + 1], ALU.add, ALU.max, maxes[b][:, c:c + 1])
                ins.then_inc(scores_read, 1)
                dve.wait_ge(scores_read, u + 1)
                link(V.tensor_scalar(neg_max[b], maxes[b], -1.0, None, ALU.mult))
                V.tensor_tensor(sink_exp[b], sinks[:, g * HG:(g + 1) * HG], neg_max[b], ALU.add).then_inc(neg_max_ready, 1)

            def rescale(u):
                b, low = u % 2, WIN if u < G else 0
                dve.wait_ge(exp_done, u + 1)
                link(V.tensor_tensor(sums[b], sums[b], sink_exp[b], ALU.add))
                link(V.reciprocal(sums[b], sums[b]))
                for c in range(HG):
                    ins = V.tensor_scalar(probs[b][:, c, low:], probs[b][:, c, low:], sums[b][:, c:c + 1], None, ALU.mult)
                ins.then_inc(probs_ready, 1)

            def att_evac(u):
                n, g = divmod(u, G)
                dve.wait_ge(task_done, done_at(("pv", u)))
                V.tensor_copy(q_sb[g * HD:(g + 1) * HD, :, n * WIN:(n + 1) * WIN],
                              task_ps[g * HD:(g + 1) * HD, :].rearrange("p (c q) -> p c q", c=HG)).then_inc(read_v, 1)
                dve.wait_ge(read_v, read_at(("pv", u)))
                dve.sem_inc(att_ready, 1)

            def bc(ap):
                return ap.unsqueeze(2).broadcast_to([ap.shape[0], NS, HG])

            def sample_task(k):
                q_s = q_sb[:, :, SEQ:].rearrange("p c b -> p b c")
                dve.wait_ge(task_done, done_at(("sample", k)))
                if k == 0:
                    V.tensor_copy(s_self, task_ps[0:32, 64:66])
                    V.tensor_copy(s_t, task_ps[:, 0:64]).then_inc(read_v, 1)
                if k == 1:
                    link(V.tensor_scalar(s_sc[:, :, WIN], s_self, SCALE, None, ALU.mult))
                    V.tensor_scalar(s_sc[:, :, 0:WIN], task_ps[0:32, 0:2 * WIN].rearrange("p (g k) -> p g k", g=G),
                                    SCALE, None, ALU.mult).then_inc(read_v, 1)
                    dve.wait_ge(read_v, read_at(("sample", 1)))
                    link(V.tensor_reduce(s_max, s_sc, mybir.AxisListType.X, ALU.max))
                    link(V.tensor_tensor(s_max, s_max, sink_s[0:32, :], ALU.max))
                    link(V.tensor_scalar(s_nmax, s_max, -1.0, None, ALU.mult))
                    V.tensor_tensor(s_esink, sink_s[0:32, :], s_nmax, ALU.add).then_inc(s_neg_ready, 1)
                    dve.wait_ge(s_exp_done, 1)
                    link(V.tensor_tensor(s_sum, s_sum, s_esink, ALU.add))
                    link(V.reciprocal(s_sum, s_sum))
                    for g in range(G):
                        link(V.tensor_scalar(s_sc[:, g, :], s_sc[:, g, :], s_sum[:, g:g + 1], None, ALU.mult))
                    for g in range(G):
                        ins = V.tensor_scalar(s_diag[:, g, :], ident[0:32, 0:32], s_sc[:, g, WIN:], None, ALU.mult)
                    ins.then_inc(s_ready, 1)
                if k == 2:
                    V.tensor_copy(s_pt, task_ps[:, 0:64])
                    V.tensor_copy(s_bc, task_ps[:, 64:96]).then_inc(read_v, 1)
                    dve.wait_ge(read_v, read_at(("sample", 2)))
                    s3 = s_bc.rearrange("p (b c) -> p b c", b=NS)
                    link(V.tensor_tensor(s3, s3, bc(vT[:, SEQ:]), ALU.mult))
                if k == 3:
                    V.tensor_tensor(q_s, task_ps[:, 0:32].rearrange("p (b c) -> p b c", b=NS),
                                    s_bc.rearrange("p (b c) -> p b c", b=NS), ALU.add).then_inc(read_v, 1)

            for j in range(OUT_JOB0):
                i, s, t = j - ATT_JOB0, j // 3, j % 3
                if j == ATT_JOB0:
                    dve.wait_ge(job_read, 18)
                    V.tensor_tensor(s_qk.rearrange("p (b c) -> p b c", b=NS), q_sb[:, :, SEQ:].rearrange("p c b -> p b c"),
                                    bc(k_sb[:, SEQ:]), ALU.mult).then_inc(s_ready, 1)
                if 1 <= i <= UNITS:
                    rescale(i - 1)
                if 0 <= i < UNITS:
                    score_max(i)
                if j in (21, 32):
                    conv_lru((j - 21) // 11)
                if j in (28, 39):
                    gate_input((j - 28) // 11)
                if j in (29, 40):
                    lru_root((j - 29) // 11)
                if j in (31, 42):
                    lru_scan((j - 31) // 11)
                if j in (36, 45):
                    sc_conv((j - 36) // 9)
                if j == 39:
                    dve.wait_ge(job_read, 39)
                    link(V.tensor_tensor(c_out[0], c_out[0], y_c, ALU.mult))
                if s == 0:
                    evac(j, k_sb)
                elif s == 1:
                    evac(j, vT)
                elif s < 6:
                    evac(j, q_sb[:, s - 2, :])
                elif s in (6, 8):
                    if t == 0:
                        V.memset(x_pad[:, 0:3], 0.0)
                        V.tensor_copy(samples(x_pad, 4)[:, :, 0:3], lru_st[:, (s - 6) // 2, :, :])
                    evac(j, x_pad[:, 3:], samples(x_pad, 4)[:, :, 3])
                elif s in (7, 9):
                    if j == 27:
                        dve.wait_ge(kv_stored, 16 * 2)
                    evac(j, g_in[(s - 7) // 2])
                elif s in (10, 13):
                    evac(j, c_out[(s - 10) // 3])
                elif s in (11, 14):
                    c = (s - 11) // 3
                    if t == 0:
                        V.memset(pad3[:, 0:2], 0.0)
                        V.tensor_copy(samples(pad3, 3)[:, :, 0:2], sc_st[:, c, :, :])
                    evac(j, pad3[:, 2:], samples(pad3, 3)[:, :, 2])
                    sc_product(c, t)
                else:
                    c = (s - 12) // 3
                    evac(j, c_out[c])
                    if c:
                        dve.wait_ge(job_read, j + 1)
                        V.tensor_tensor(c_out[1][:, tile(t)], c_out[1][:, tile(t)], y_c[:, tile(t)],
                                        ALU.mult).then_inc(c_ready, 1)
                if j == 44:
                    pass
                if j == 45:
                    dve.sem_inc(scratch_free, 1)
                if 2 <= i <= UNITS + 1:
                    att_evac(i - 2)
                for name, _ in AFTER.get(j, []):
                    if name[0] == "v":
                        dve.wait_ge(task_done, done_at(name))
                        V.tensor_copy(v_tok[:, 4 * name[1]:4 * name[1] + 4, :],
                                      task_ps[:, :].rearrange("p (n d) -> p n d", n=4)).then_inc(read_v, 1)
                    if name[0] == "sample":
                        sample_task(name[1])
                if j in A_STEPS:
                    sq_tree(("norm", "A", A_STEPS.index(j)), HG)
                if 38 <= j < 41:
                    reciprocal(("norm", "A", j - 38), k_sb[:, tile(j - 38)])
                if j == 41:
                    for k in range(HG):
                        V.scalar_tensor_tensor(out=q_sb[:, k, :], in0=q_sb[:, k, :], scalar=gain_out[:, k:k + 1], in1=k_sb,
                                               op0=ALU.mult, op1=ALU.mult).then_inc(ab_ready, 1)
                if j in B_STEPS:
                    sq_tree(("norm", "B", B_STEPS.index(j)), 2)
                if 45 <= j < 48:
                    reciprocal(("norm", "B", j - 45), zb[:, 5, tile(j - 45)])
            for c in range(2):
                V.scalar_tensor_tensor(out=b_out[c], in0=b_out[c], scalar=gain_out[:, 4 + c:5 + c], in1=zb[:, 5, :],
                                       op0=ALU.mult, op1=ALU.mult).then_inc(ab_ready, 1)

            def merged_ab(t):
                dve.wait_ge(h_hi_ready, NT + 2 * t + 1)
                for k in range(6):
                    ins = V.tensor_tensor(h_lo[:, k, tile(t)], zb[:, (k if k < 4 else k + 2), tile(t)],
                                          f32(h_hi[:, k, tile(t)]), ALU.subtract)
                ins.then_inc(h_ready, 1)

            def merged_c(t):
                reciprocal(("norm", "C", t), k_sb[:, tile(t)])
                for c in range(2):
                    ins = V.scalar_tensor_tensor(out=c_out[c][:, tile(t)], in0=c_out[c][:, tile(t)],
                                                 scalar=gain_out[:, 6 + c:7 + c], in1=k_sb[:, tile(t)],
                                                 op0=ALU.mult, op1=ALU.mult)
                ins.then_inc(cm_ready, 1)
                dve.wait_ge(cm_ready, t + 1)
                dve.wait_ge(h_hi_ready, NT + 2 * t + 2)
                for k in range(2):
                    ins = V.tensor_tensor(h_lo[:, 6 + k, tile(t)], c_out[k][:, tile(t)],
                                          f32(h_hi[:, 6 + k, tile(t)]), ALU.subtract)
                ins.then_inc(h_ready, 1)

            def w_lo2(s):
                dve.wait_ge(w_hi_ready, s + 1)
                w = slice(KD * P // 2, KD * P)
                V.tensor_tensor(w_lo[s % SPLIT][:, w], raw[s % RAW][:, w], f32(w_hi[s % SPLIT][:, w]),
                                ALU.subtract).then_inc(w_lo2_ready, 1)

            def out_evac(j):
                t, m = divmod(j, KD)
                dve.wait_ge(job_done, OUT_JOB0 + j + 1)
                dve.wait_ge(x_back[m], 16)
                V.tensor_tensor(x_sb[:, m, tile(t)], job_ps[(OUT_JOB0 + j) % 3], x_sb[:, m, tile(t)],
                                ALU.add).then_inc(job_read, 1)

            def x2_split(t):
                dve.wait_ge(h_hi_ready, 9 + t + 1)
                for k in range(KD):
                    ins = V.scalar_tensor_tensor(out=h_lo[:, k, tile(t)], in0=x_sb[:, k, tile(t)],
                                                 scalar=gain_ffn[:, k:k + 1], in1=f32(h_hi[:, k, tile(t)]),
                                                 op0=ALU.mult, op1=ALU.subtract)
                ins.then_inc(h_ready, 1)

            sq_tree(("norm", "C", 0), 2)
            w_lo2(OUT_SLOT0)
            merged_ab(0)
            merged_c(0)
            for j in range(NT * KD):
                if j + 1 < NT * KD:
                    w_lo2(OUT_SLOT0 + j + 1)
                out_evac(j)
                if j == 0:
                    sq_tree(("norm", "C", 1), 2)
                    merged_ab(1)
                if j == 1:
                    merged_c(1)
                if j == 3:
                    sq_tree(("norm", "C", 2), 2)
                    merged_ab(2)
                if j == 4:
                    merged_c(2)
                if j in (KD + 1, 2 * KD + 1):
                    x2_split(j // KD - 1)
                    sq_tree(("norm", "X", j // KD - 1), KD)
                if j in (KD + 3, 2 * KD + 3):
                    reciprocal(("norm", "X", j // KD - 1), rstd[:, tile(j // KD - 1)])
            x2_split(2)
            sq_tree(("norm", "X", 2), KD)

            V.memset(pad_g[:, 0:2], 0.0)
            V.memset(pad_u[:, 0:2], 0.0)

            def ffn_evac(job, t, pad, i):
                dve.wait_ge(job_done, job + 1 if i is None else i * 12 + (job + 1))
                src, scale = job_ps[t], rstd[:, tile(t)]
                if t < NT - 1:
                    V.tensor_tensor(pad[:, 2 + t * TW:2 + (t + 1) * TW], src, scale, ALU.mult).then_inc(job_read, 1)
                else:
                    V.tensor_tensor(pad[:, 2 + t * TW:2 + SEQ], src[:, 0:LAST], scale[:, 0:LAST], ALU.mult)
                    V.tensor_tensor(samples(pad, 3)[:, :, 2], src[:, LAST:], scale[:, LAST:], ALU.mult).then_inc(job_read, 1)
                    dve.wait_ge(job_read, job + 1 if i is None else i * 12 + (job + 1))

            def ffn_half(job, c, pad, out, i, before_last=None):
                def col(n, k=0, w=1):
                    return slice(n * c + k, n * c + k + w) if i is None else bass.ds(i * (4 * n) + (n * c + k), w)

                s = samples(pad, 3)
                V.tensor_copy(s[:, :, 0:2], ffn_st[:, col(16, 0, 16)].rearrange("p (b k) -> p b k", b=NS))
                for t in range(NT):
                    if t == NT - 1 and before_last:
                        before_last()
                    ffn_evac(job + t, t, pad, i)
                V.tensor_copy(ffn_tail[:, col(2, 0, 2)], pad[:, SEQ:SEQ + 2])
                V.tensor_copy(ffn_st[:, col(16, 0, 16)].rearrange("p (b k) -> p b k", b=NS), s[:, :, 1:3])
                return conv3(pad, lambda k: ffn_cw[:, col(3, k)], conv_tmp, out)

            conv_tmp = zflat[:, 5500:5500 + YC]
            yg_c, yu_c = y_g[:, 0:T], y_u[:, 0:T]

            def ffn_chunk(n, job, i=None, before_last=None):
                ffn_half(job, 2 * n, pad_g, yg_c, i, before_last).then_inc(conv_g_ready, 1)
                link(ffn_half(job + 3, 2 * n + 1, pad_u, yu_c, i))
                dve.wait_ge(silu_done, n + 1 if i is None else i * 2 + (n + 1))
                V.tensor_tensor(act_f, yg_c, yu_c, ALU.mult).then_inc(act_ready, 1)

            def act_rest(n, i=None):
                dve.wait_ge(act_hi_ready, n + 1 if i is None else i * 2 + (n + 1))
                V.tensor_tensor(act_lo[n % 2][:, :], act_f, f32(act_hi[n % 2][:, :]), ALU.subtract).then_inc(act_split, 1)

            def down_evac(d, i=None):
                half_, t, m = d // 12, d % 12 // 4, d % 4
                dve.wait_ge(down_done, d + 1 if i is None else i * 24 + (d + 1))
                m += 4 * half_
                V.tensor_tensor(x_sb[:, m, tile(t)], down_ps[d % 4], x_sb[:, m, tile(t)], ALU.add).then_inc(down_read, 1)

            ffn_chunk(0, FFN_JOB0, before_last=lambda: reciprocal(("norm", "X", 2), rstd[:, tile(2)]))
            act_rest(0)
            ffn_chunk(1, FFN_JOB0 + 6)
            act_rest(1)
            with dve.Fori(0, LOOPS) as i:
                link.enter(i, 10)
                ffn_chunk(2, LOOP_JOB0, i)
                for d in range(24):
                    down_evac(d, i)
                act_rest(2, i)
                ffn_chunk(3, LOOP_JOB0 + 6, i)
                act_rest(3, i)
                link.leave(LOOPS)
            for d in range(24):
                n = 24 * LOOPS + d
                half_, t, m = d // 12, d % 12 // 4, d % 4
                dve.wait_ge(down_done, n + 1)
                m += 4 * half_
                V.tensor_tensor(x_sb[:, m, tile(t)], down_ps[d % 4], x_sb[:, m, tile(t)], ALU.add).then_inc(down_read, 1)
                if d == 23:
                    for t in range(NT):
                        sq_tree(("norm", "F", t), KD)
                        reciprocal(("norm", "F", t), rstd[:, tile(t)])
                        for m in range(KD):
                            ins = V.scalar_tensor_tensor(out=x_sb[:, m, tile(t)], in0=x_sb[:, m, tile(t)],
                                                         scalar=gain_fin[:, m:m + 1], in1=rstd[:, tile(t)],
                                                         op0=ALU.mult, op1=ALU.mult)
                        ins.then_inc(y_ready, 1)

        @block.tensor
        def _(pe):
            mm = nc.tensor.matmul

            def passes(out, chunks):
                n = 3 * len(chunks)
                at = 0
                for wh, wl, xh, xl in chunks:
                    for a, b in ((wh, xh), (wh, xl), (wl, xh)):
                        ins = mm(out, a, b, start=(at == 0), stop=(at == n - 1))
                        at += 1
                return ins

            def wslot(s, k):
                cols = slice(k * P, (k + 1) * P)
                return w_hi[s % SPLIT][:, cols], w_lo[s % SPLIT][:, cols]

            def job(j, s, t, i=None):
                if i is None:
                    pe.wait_ge(w_lo_ready, s + 1)
                    if j >= 3:
                        pe.wait_ge(job_read, j - 2)
                else:
                    pe.wait_ge(w_lo_ready, i * PER_SLOT + (s + 1))
                    pe.wait_ge(job_read, i * 12 + (j - 2))
                return passes(job_ps[t], [(*wslot(s, k), h_hi[:, k, tile(t)], h_lo[:, k, tile(t)]) for k in range(KD)])

            def task(name):
                n = TASK[name]
                if n:
                    before, reader = ORDER[n - 1]
                    pe.wait_ge(read_a if reader == "A" else read_v, read_at(before))
                kind = name[0]
                if kind == "norm":
                    pe.wait_ge(sq_sum_ready, NORMS.index(name) + 1)
                    ins = mm(task_ps[:, 0:TW], ones[:, :], sq[:, 0, :], start=True, stop=True)
                if kind == "v":
                    for b in range(4):
                        n = 4 * name[1] + b
                        ins = nc.tensor.transpose(task_ps[:, b * P:(b + 1) * P], vT[:, n * WIN:(n + 1) * WIN], ident[:, :])
                if kind == "gate":
                    _, c, k = name
                    pe.wait_ge(xc_ready, c + 1)
                    pe.wait_ge(gate_landed, 16 * 8)
                    w = gate_w[:, (k // 3 * 2 + c) * P:(k // 3 * 2 + c + 1) * P]
                    ins = mm(task_ps[:, 0:TW], w, xc[:, tile(k % 3)], start=True, stop=True)
                if kind == "pv":
                    u = name[1]
                    n, g = divmod(u, G)
                    pe.wait_ge(probs_t_ready, u + 1)
                    out = task_ps[g * HD:(g + 1) * HD, :]
                    blocks = [1] if n == 0 else [0, 1]
                    for s in blocks:
                        ins = mm(out, v_tok[:, n - 1 + s, g * HD:(g + 1) * HD], probs_t[:, s, :],
                                 start=(s == blocks[0]), stop=(s == 1))
                if kind == "sample":
                    sample(name[1]).then_inc(task_done, 1)
                    return
                ins.then_inc(task_done, 1)

            def sample(k):
                if k == 0:
                    pe.wait_ge(s_ready, 1)
                    pe.wait_ge(cache_landed, 32)
                    for g in range(G):
                        rows = slice(g * HD, (g + 1) * HD)
                        for b in range(NS):
                            o = g * 32 + b * HG
                            ins = mm(task_ps[:, o:o + HG], ck[rows, b, :], q_sb[rows, :, SEQ + b], start=True, stop=True)
                        ins.then_inc(pe_link, 1)
                        pe.wait_ge(pe_link, g + 1)
                    return mm(task_ps[0:32, 64:66], s_qk, half[:, :], start=True, stop=True)
                if k == 1:
                    for g in range(G):
                        ins = nc.tensor.transpose(task_ps[0:32, g * WIN:(g + 1) * WIN], s_t[:, g * 32:(g + 1) * 32], ident[:, :])
                    return ins
                if k == 2:
                    pe.wait_ge(s_ready, 2)
                    for g in range(G):
                        nc.tensor.transpose(task_ps[:, g * 32:(g + 1) * 32], s_sc[:, g, 0:WIN], ident[0:32, 0:32])
                    for g in range(G):
                        ins = mm(task_ps[g * HD:(g + 1) * HD, 64:96], ones[0:32, 0:HD], s_diag[:, g, :], start=True, stop=True)
                    return ins
                for g in range(G):
                    for b in range(NS):
                        o = b * HG
                        ins = mm(task_ps[g * HD:(g + 1) * HD, o:o + HG], cv[:, b, g * HD:(g + 1) * HD],
                                 s_pt[:, g * 32 + o:g * 32 + o + HG], start=True, stop=True)
                return ins

            def scores(u):
                n, g = divmod(u, G)
                rows = slice(g * HD, (g + 1) * HD)
                low = WIN if n == 0 else 0
                if u:
                    pe.wait_ge(scores_read, u)
                for c in range(HG):
                    ins = mm(score_ps[:, c, low:], q_sb[rows, c, n * WIN:(n + 1) * WIN],
                             k_sb[rows, (n - 1) * WIN + low:(n + 1) * WIN], start=True, stop=True)
                ins.then_inc(scores_done, 1)

            def transposes(u):
                pe.wait_ge(probs_ready, u + 1)
                if u:
                    pe.wait_ge(probs_t_ready, u)
                for s in ([1] if u < G else [0, 1]):
                    for c in range(HG):
                        ins = nc.tensor.transpose(trans_ps[:, s, c * WIN:(c + 1) * WIN],
                                                  probs[u % 2][:, c, s * WIN:(s + 1) * WIN], ident[:, :])
                ins.then_inc(trans_done, 1)

            pe.wait_ge(consts_made, 4)
            for j in range(OUT_JOB0):
                s, t = divmod(j, NT)
                i = j - ATT_JOB0
                if j < NT:
                    pe.wait_ge(h_ready, t + 1)
                if i == 0:
                    pe.wait_ge(job_read, 18)
                if 0 <= i < UNITS:
                    scores(i)
                job(j, s, t).then_inc(job_done, 1)
                if t == NT - 1:
                    pe.wait_ge(job_done, j + 1)
                    pe.sem_inc(w_used, 1)
                if j == 6:
                    pe.wait_ge(job_read, 6)
                for name, _ in AFTER.get(j, []):
                    task(name)
                if 1 <= i <= UNITS:
                    transposes(i - 1)

            for j in range(NT * KD):
                t, m = divmod(j, KD)
                s = OUT_SLOT0 + j
                J = OUT_JOB0 + j
                pe.wait_ge(w_lo_ready, s + 1)
                pe.wait_ge(w_lo2_ready, j + 1)
                pe.wait_ge(job_read, J - 2)
                if m == 0:
                    pe.wait_ge(h_ready, NT + 2 * t + 1)
                xs = lambda k: (h_hi[:, k, tile(t)], h_lo[:, k, tile(t)])
                out = job_ps[J % 3]
                at = 0
                for k in range(KD):
                    if m == 0 and k == 6:
                        pe.wait_ge(h_ready, NT + 2 * t + 2)
                    wh, wl = wslot(s, k)
                    xh, xl = xs(k)
                    for a, b in ((wh, xh), (wh, xl), (wl, xh)):
                        ins = mm(out, a, b, start=(at == 0), stop=(at == 3 * KD - 1))
                        at += 1
                ins.then_inc(job_done, 1)
                pe.wait_ge(job_done, J + 1)
                pe.sem_inc(w_used, 1)
                for name, _ in AFTER.get(J, []):
                    task(name)

            def up_slot(j, s, i=None, first=False):
                for t in range(NT):
                    if first:
                        pe.wait_ge(h_ready, 9 + t + 1)
                    job(j + t, s, t, i).then_inc(job_done, 1)
                    if first:
                        for name, _ in AFTER.get(j + t, []):
                            task(name)
                used(j + NT, i, 12, job_done)

            def used(n, i, per, done):
                pe.wait_ge(done, n if i is None else i * per + n)
                pe.sem_inc(w_used, 1)

            def down_slot(h, s, i=None, base=0, between=None):
                pe.wait_ge(w_lo_ready, s + 1 if i is None else i * PER_SLOT + (s + 1))
                for d in range(12 * h, 12 * h + 12):
                    t, m = d % 12 // 4, d % 4
                    n = base + d
                    if i is None or d >= 4:
                        pe.wait_ge(down_read, n - 3 if i is None else i * 24 + (n - 3))
                    elif d < 4:
                        pe.wait_ge(down_read, i * 24)
                    passes(down_ps[d % 4], [(*wslot(s, kk * 4 + m), act_hi[kk][:, tile(t)], act_lo[kk][:, tile(t)])
                                            for kk in range(2)]).then_inc(down_done, 1)
                used(base + 12 * h + 12, i, 24, down_done)

            up_slot(FFN_JOB0, FFN_SLOT0, first=True)
            for c in range(1, 4):
                up_slot(FFN_JOB0 + 3 * c, FFN_SLOT0 + c)
            with pe.Fori(0, LOOPS) as i:
                up_slot(LOOP_JOB0, LOOP_SLOT0, i)
                up_slot(LOOP_JOB0 + 3, LOOP_SLOT0 + 1, i)
                pe.wait_ge(act_split, i * 2 + 2)
                down_slot(0, LOOP_SLOT0 + 2, i)
                down_slot(1, LOOP_SLOT0 + 3, i)
                up_slot(LOOP_JOB0 + 6, LOOP_SLOT0 + 4, i)
                up_slot(LOOP_JOB0 + 9, LOOP_SLOT0 + 5, i)
            pe.wait_ge(act_split, NF)
            down_slot(0, LAST_SLOT0, base=24 * LOOPS)
            down_slot(1, LAST_SLOT0 + 1, base=24 * LOOPS)
            for t in range(NT):
                task(("norm", "F", t))


def x2_split_hi(nc, act, t, h_hi, x_sb, gain, tile, job_read, h_hi_ready):
    act.wait_ge(job_read, OUT_JOB0 + KD * (t + 1))
    for k in range(KD):
        ins = nc.scalar.activation(h_hi[:, k, tile(t)], x_sb[:, k, tile(t)], ACT.Copy, scale=gain[:, k:k + 1])
    ins.then_inc(h_hi_ready, 1)


_OUTS = {
    "y": (P, KD, T), "k_new": (P, WIN + NS), "v_new": (P, WIN + NS), "k_old": (NS, WIN - 1, P), "v_old": (NS, WIN - 1, P),
    "h_last": (P, 2, NS + 1), "lru_state": (P, 2, 3 + 3 * NS), "sc_state": (P, 2, 2 + 2 * NS),
    "ffn_tail": (P, 2 * NF * 2), "ffn_sample": (P, 2 * NF * 16),
}


def _blocks(w):
    k, m = w.shape
    return w.reshape(k // P, P, m // P, P).transpose(2, 1, 0, 3).reshape(m // P, P, k // P * P)


def _rows(v):
    v = np.moveaxis(v, -1, 0)
    return np.moveaxis(v.reshape(v.shape[0] // P, P, *v.shape[1:]), 1, 0)


def kernel(**inputs):
    import concourse.bacc as bacc
    from concourse.bass_utils import run_bass_kernel_spmd as run

    a = {k: np.asarray(v) for k, v in inputs.items()}
    head = np.arange(512).reshape(2, HG, HD).transpose(1, 0, 2).reshape(-1)
    cols = np.arange(2048)
    q, k, v, lx, lg, sb_, sc_, su = (cols[i:j] for i, j in
                                     ((0, 512), (512, 640), (640, 768), (768, 1024), (1024, 1280), (1280, 1536), (1536, 1792), (1792, 2048)))
    order = np.concatenate([k, v, q[head], lx[:P], lg[:P], lx[P:], lg[P:], sc_[:P], su[:P], sb_[:P], sc_[P:], su[P:], sb_[P:]])
    rows = np.concatenate([head, np.arange(512, 1024)])
    w_in, w_out, w_up, w_down = (a[n][0] for n in ("w_in", "w_out", "w_up", "w_down"))
    ff = np.arange(2 * FF).reshape(2, NF, P)[::-1].transpose(1, 0, 2).reshape(-1)
    up = _blocks(w_up[:, ff]).reshape(NG, 4, P, D)
    down = w_down.reshape(NG, 2, P, 2, 4, P).transpose(0, 3, 2, 1, 4, 5).reshape(NG, 2, P, D)
    slots = [up[0]]
    for g in range(1, NG):
        slots += [up[g, 0:2], down[g - 1], up[g, 2:4]]
    slots.append(down[NG - 1])
    w = np.concatenate([_blocks(w_in[:, order]), _blocks(w_out[rows])] + slots)
    x = np.concatenate([a["x_prompt"][0], a["x_sample"][:, 0]]).T.reshape(KD, P, T).transpose(1, 0, 2)
    sinks = a["sinks"][0]
    sink_s = np.zeros((P, 2), np.float32)
    sink_s[0:32] = np.tile(sinks.reshape(G, HG).T, (NS, 1))
    const = np.concatenate([z.reshape(P, -1) for z in (
        _rows(a["g_mix"][0]), _rows(a["g_out"][0][rows]), _rows(a["g_ffn"][0]), _rows(a["g_final"]),
        np.broadcast_to(sinks, (P, 8)),
        _rows(a["lru_conv_w"][0]), _rows(a["lru_conv_b"][0]), _rows(a["lru_ba"][0]), _rows(a["lru_bi"][0]), _rows(a["lru_lambda"][0]),
        _rows(a["sc_conv_w"][0]), _rows(a["state_lru_conv"][0]), _rows(a["state_rglru"][0]), _rows(a["state_sconv"][0]),
        sink_s, _rows(a["ffn_conv_w"][0][:, ff]))], axis=1)
    arrays = {
        "x": x, "w": w, "const": const, "ffn_state": _rows(a["state_ffn_conv"][0][:, :, ff]).reshape(P, -1),
        "gate_w": np.stack([a["lru_wa"][0], a["lru_wi"][0]]),
        "ck": a["cache_k"][0].transpose(2, 3, 0, 1).reshape(P, NS, WIN), "cv": a["cache_v"][0].reshape(NS, WIN, P).transpose(1, 0, 2),
        "k_keep": a["cache_k"][0].reshape(NS, WIN, P)[:, 1:], "v_keep": a["cache_v"][0].reshape(NS, WIN, P)[:, 1:],
    }
    arrays = {f"in_{n}": np.ascontiguousarray(z) for n, z in arrays.items()}
    nc = bacc.Bacc("TRN2", target_bir_lowering=False, num_devices=1)
    dram = {n[3:]: nc.dram_tensor(n, z.shape, F32, kind="ExternalInput").ap() for n, z in arrays.items()}
    outs = {n: nc.dram_tensor(f"out_{n}", s, F32, kind="ExternalOutput").ap() for n, s in _OUTS.items()}
    build(nc, dram, outs)
    r = run(nc, [arrays], core_ids=[0]).results[0]
    o = {n: np.asarray(r[f"out_{n}"]) for n in _OUTS}

    y = o["y"].transpose(2, 1, 0).reshape(T, D)
    back = np.argsort(ff)

    def feat(z):
        z = np.moveaxis(z, 0, 1)
        return np.moveaxis(z.reshape(-1, *z.shape[2:]), 0, -1)

    def cache(old, new):
        rows_ = new[:, WIN:].T.reshape(NS, 1, P)
        return np.concatenate([old, rows_], axis=1).reshape(1, NS, WIN, G, HD)

    hl, ls, ss = feat(o["h_last"]), feat(o["lru_state"]), feat(o["sc_state"])
    ft = feat(o["ffn_tail"].reshape(P, 2 * NF, 2))[:, back]
    fs = feat(o["ffn_sample"].reshape(P, 2 * NF, NS, 2))[:, :, back]
    return (
        y[None, :SEQ], y[SEQ:, None],
        o["k_new"][:, :WIN].T.reshape(1, 1, WIN, G, HD), o["v_new"][:, :WIN].T.reshape(1, 1, WIN, G, HD),
        hl[None, 0:1], ls[None, None, 0:3], ss[None, None, 0:2], ft[None, None],
        cache(o["k_old"], o["k_new"]), cache(o["v_old"], o["v_new"]),
        hl[None, 1:], ls[3:].reshape(1, NS, 3, 2 * P), ss[2:].reshape(1, NS, 2, 2 * P), fs[None],
    )
```
